# Optimizing a Trainium2 kernel written in Bass

```python
import math
import jax, jax.numpy as jnp
from jax import lax
import numpy as np

D_MODEL = 1024
BATCH = 1
SEQ = 512
DEPTH = 2

BRANCH_WIDTH = 512
N_BRANCH = 3
EPS = 1e-6
NEG_BIG = -1e30
HG_HEADS = 4
HG_DIM = 128
HG_CHUNK = 64
AT_HEADS = 4
AT_DIM = 128
IDX_HEADS = 8
IDX_DIM = 64
TOPK_MAX = 256
Q_BLOCK = 128
ROPE_THETA = 10000.0
S5_GROUP = 16
S5_GROUPS = BRANCH_WIDTH // S5_GROUP
S5_STATE = 64

IN_SPLITS = (
    HG_HEADS * HG_DIM, HG_HEADS * HG_DIM, HG_HEADS * HG_DIM, BRANCH_WIDTH,
    AT_HEADS * AT_DIM, AT_DIM, AT_DIM, BRANCH_WIDTH,
    IDX_HEADS * IDX_DIM, IDX_DIM, IDX_HEADS,
    BRANCH_WIDTH, BRANCH_WIDTH,
    N_BRANCH * D_MODEL,
)
N_IN = 4 * BRANCH_WIDTH + (2 * BRANCH_WIDTH + 2 * AT_DIM) + (IDX_HEADS * IDX_DIM + IDX_DIM + IDX_HEADS) + 2 * BRANCH_WIDTH + N_BRANCH * D_MODEL

kernel_name = "hybrid_hgrn2_dsa_s5_gated_trunk"

def rms_norm(x, g):
    x32 = x.astype(jnp.float32)
    r = lax.rsqrt(jnp.mean(x32 * x32, axis=-1, keepdims=True) + EPS)
    return (x32 * r).astype(x.dtype) * g

def rope_tables(positions, dim):
    inv_freq = ROPE_THETA ** (-jnp.arange(0, dim, 2, dtype=jnp.float32) / dim)
    ang = positions.astype(jnp.float32)[..., None] * inv_freq
    return jnp.cos(ang)[:, :, None, :], jnp.sin(ang)[:, :, None, :]

def apply_rope(x, cos, sin):
    half = x.shape[-1] // 2
    x1 = x[..., :half].astype(jnp.float32)
    x2 = x[..., half:].astype(jnp.float32)
    out = jnp.concatenate([x1 * cos - x2 * sin, x2 * cos + x1 * sin], axis=-1)
    return out.astype(x.dtype)

def split_cols(p):
    out = []
    o = 0
    for n in IN_SPLITS:
        out.append(p[..., o:o + n])
        o += n
    return out

def hgrn2_mixer(q, fz, i, lb, onorm_g):
    B, S, W = q.shape
    C = HG_CHUNK
    NC = S // C
    lb = lb.astype(jnp.float32)
    sg = jax.nn.sigmoid(fz.astype(jnp.float32))
    f = lb + (1.0 - lb) * sg
    log_f = jnp.log(jnp.maximum(f, 1e-30))
    k = 1.0 - f

    def to_chunks(a):
        return a.astype(jnp.float32).reshape(B, NC, C, HG_HEADS, HG_DIM).transpose(1, 0, 3, 2, 4)

    tri = jnp.tril(jnp.ones((C, C), dtype=bool))[None, None, :, :, None]

    def step(state, inp):
        qc, kc, vc, lfc = inp
        b = jnp.cumsum(lfc, axis=2)
        o_inter = jnp.einsum('bhtd,bhde->bhte', qc * jnp.exp(b), state)
        diff = b[:, :, :, None, :] - b[:, :, None, :, :]
        decay = jnp.where(tri, jnp.exp(jnp.where(tri, diff, 0.0)), 0.0)
        scores = jnp.einsum('bhtd,bhsd,bhtsd->bhts', qc, kc, decay)
        o_intra = jnp.einsum('bhts,bhse->bhte', scores, vc)
        b_last = b[:, :, -1:, :]
        k_dec = kc * jnp.exp(b_last - b)
        state = jnp.exp(b_last[:, :, 0, :])[..., None] * state + jnp.einsum('bhsd,bhse->bhde', k_dec, vc)
        return state, o_inter + o_intra

    state0 = jnp.zeros((B, HG_HEADS, HG_DIM, HG_DIM), jnp.float32)
    _, o = lax.scan(step, state0, (to_chunks(q), to_chunks(k), to_chunks(i), to_chunks(log_f)))
    o = o.transpose(1, 0, 3, 2, 4).reshape(B, S, HG_HEADS, HG_DIM).astype(q.dtype)
    o = rms_norm(o, onorm_g)
    return o.reshape(B, S, W)

def dsa_mixer(q, k, v, iq, ik, iw, positions, qn_g, kn_g):
    B, S, _ = q.shape
    topk = min(TOPK_MAX, S // 4)
    NB = S // Q_BLOCK
    cos, sin = rope_tables(positions, AT_DIM)
    cos_i, sin_i = rope_tables(positions, IDX_DIM)
    q = apply_rope(rms_norm(q.reshape(B, S, AT_HEADS, AT_DIM), qn_g), cos, sin)
    k = apply_rope(rms_norm(k[:, :, None, :], kn_g), cos, sin)[:, :, 0, :]
    iq = apply_rope(iq.reshape(B, S, IDX_HEADS, IDX_DIM), cos_i, sin_i)
    ik = apply_rope(ik[:, :, None, :], cos_i, sin_i)[:, :, 0, :]
    scale = 1.0 / math.sqrt(AT_DIM)
    key_pos = jnp.arange(S)

    def blocks(a):
        return jnp.moveaxis(a.reshape((B, NB, Q_BLOCK) + a.shape[2:]), 1, 0)

    def one_block(args):
        qb, iqb, iwb, blk = args
        qpos = blk * Q_BLOCK + jnp.arange(Q_BLOCK)
        rel = jax.nn.relu(jnp.einsum('bqhd,bsd->bqhs', iqb, ik).astype(jnp.float32))
        isc = jnp.einsum('bqhs,bqh->bqs', rel, iwb.astype(jnp.float32))
        causal = key_pos[None, :] <= qpos[:, None]
        isc = jnp.where(causal[None], isc, NEG_BIG)
        _, idx = lax.top_k(isc, topk)
        ksel = jax.vmap(lambda kk, ii: kk[ii])(k, idx)
        vsel = jax.vmap(lambda vv, ii: vv[ii])(v, idx)
        logits = jnp.einsum('bqhd,bqkd->bqhk', qb, ksel).astype(jnp.float32) * scale
        valid = idx <= qpos[None, :, None]
        logits = jnp.where(valid[:, :, None, :], logits, NEG_BIG)
        p = jax.nn.softmax(logits, axis=-1).astype(v.dtype)
        return jnp.einsum('bqhk,bqkd->bqhd', p, vsel)

    out = lax.map(one_block, (blocks(q), blocks(iq), blocks(iw), jnp.arange(NB)))
    return jnp.moveaxis(out, 0, 1).reshape(B, S, AT_HEADS * AT_DIM)

def s5_mixer(u, a_re, a_im, log_dt, b_re, b_im, c_re, c_im, d_skip, glu_w, glu_b):
    B, S, W = u.shape
    f32 = jnp.float32
    ug = u.astype(f32).reshape(B, S, S5_GROUPS, S5_GROUP)
    a_re = a_re.astype(f32); a_im = a_im.astype(f32)
    dt = jnp.exp(log_dt.astype(f32))[:, None]
    mag = jnp.exp(a_re * dt)
    ang = a_im * dt
    abar_re = mag * jnp.cos(ang)
    abar_im = mag * jnp.sin(ang)
    nr = abar_re - 1.0
    ni = abar_im
    den = a_re * a_re + a_im * a_im
    fr = (nr * a_re + ni * a_im) / den
    fi = (ni * a_re - nr * a_im) / den
    b_re = b_re.astype(f32); b_im = b_im.astype(f32)
    bbar_re = fr[..., None] * b_re - fi[..., None] * b_im
    bbar_im = fr[..., None] * b_im + fi[..., None] * b_re
    bu_re = jnp.einsum('bsgc,gpc->bsgp', ug, bbar_re)
    bu_im = jnp.einsum('bsgc,gpc->bsgp', ug, bbar_im)
    ar_t = jnp.broadcast_to(abar_re, bu_re.shape)
    ai_t = jnp.broadcast_to(abar_im, bu_re.shape)

    def combine(e1, e2):
        a1r, a1i, b1r, b1i = e1
        a2r, a2i, b2r, b2i = e2
        return (a2r * a1r - a2i * a1i,
                a2r * a1i + a2i * a1r,
                a2r * b1r - a2i * b1i + b2r,
                a2r * b1i + a2i * b1r + b2i)

    _, _, xr, xi = lax.associative_scan(combine, (ar_t, ai_t, bu_re, bu_im), axis=1)
    y = (jnp.einsum('gcp,bsgp->bsgc', c_re.astype(f32), xr)
         - jnp.einsum('gcp,bsgp->bsgc', c_im.astype(f32), xi))
    y = y.reshape(B, S, W) + d_skip.astype(f32) * u.astype(f32)
    y = jax.nn.gelu(y).astype(u.dtype)
    return y * jax.nn.sigmoid(y @ glu_w + glu_b)

def hybrid_layer(x, c, lb, ada_w, ada_b, norm_g, w_in, hg_onorm_g, at_qnorm_g, at_knorm_g,
                 s5_a_re, s5_a_im, s5_log_dt, s5_b_re, s5_b_im, s5_c_re, s5_c_im, s5_d,
                 s5_glu_w, s5_glu_b, w_branch, w_out, positions):
    B, S, D = x.shape
    mod = jax.nn.silu(c) @ ada_w + ada_b
    shift, scale, gate = jnp.split(mod[:, None, :], 3, axis=-1)
    h = rms_norm(x, norm_g) * (1.0 + scale) + shift
    proj = h @ w_in
    (hg_q, hg_f, hg_i, hg_g, at_q, at_k, at_v, at_g,
     ix_q, ix_k, ix_w, s5_u, s5_g, merge_g) = split_cols(proj)
    ya = hgrn2_mixer(hg_q, hg_f, hg_i, lb, hg_onorm_g) * jax.nn.silu(hg_g)
    yb = dsa_mixer(at_q, at_k, at_v, ix_q, ix_k, ix_w, positions, at_qnorm_g, at_knorm_g) * jax.nn.silu(at_g)
    yc = s5_mixer(s5_u, s5_a_re, s5_a_im, s5_log_dt, s5_b_re, s5_b_im, s5_c_re, s5_c_im,
                  s5_d, s5_glu_w, s5_glu_b) * jax.nn.silu(s5_g)
    ys = jnp.stack([ya, yb, yc], axis=2)
    yd = jnp.einsum('bsnw,nwd->bsnd', ys, w_branch)
    gates = jax.nn.sigmoid(merge_g).reshape(B, S, N_BRANCH, D)
    merged = jnp.einsum('bsnd,bsnd->bsd', gates, yd)
    return x + gate * (merged @ w_out)

def setup_inputs(seed: int = 0) -> dict:
    key = jax.random.key(seed)
    ks = jax.random.split(key, 26)
    f32 = jnp.float32
    L, D, W, G, P = DEPTH, D_MODEL, BRANCH_WIDTH, S5_GROUPS, S5_STATE
    nrm = lambda k, shape, s: jax.random.normal(k, shape, f32) * s
    x = nrm(ks[0], (BATCH, SEQ, D), 1.0)
    c = nrm(ks[1], (BATCH, D), 1.0)
    offsets = jax.random.randint(ks[2], (BATCH, 1), 0, 1024, dtype=jnp.int32)
    positions = (offsets + jnp.arange(SEQ, dtype=jnp.int32)[None, :]).astype(jnp.int32)
    n_idx = jnp.arange(P, dtype=f32)
    return {
        "x": x,
        "c": c,
        "positions": positions,
        "ada_w": nrm(ks[3], (L, D, 3 * D), 0.5 * D ** -0.5),
        "ada_b": nrm(ks[4], (L, 3 * D), 0.02),
        "norm_g": 1.0 + nrm(ks[5], (L, D), 0.01),
        "w_in": nrm(ks[6], (L, D, N_IN), D ** -0.5),
        "hg_lb_logits": nrm(ks[7], (L, HG_HEADS * HG_DIM), 0.1),
        "hg_onorm_g": 1.0 + nrm(ks[8], (L, HG_DIM), 0.01),
        "at_qnorm_g": 1.0 + nrm(ks[9], (L, AT_DIM), 0.01),
        "at_knorm_g": 1.0 + nrm(ks[10], (L, AT_DIM), 0.01),
        "s5_a_re": -0.5 + nrm(ks[11], (L, G, P), 0.01),
        "s5_a_im": math.pi * n_idx[None, None, :] + nrm(ks[12], (L, G, P), 0.01),
        "s5_log_dt": jax.random.uniform(ks[13], (L, G), f32, math.log(1e-3), math.log(1e-1)),
        "s5_b_re": nrm(ks[14], (L, G, P, S5_GROUP), (2.0 * S5_GROUP) ** -0.5),
        "s5_b_im": nrm(ks[15], (L, G, P, S5_GROUP), (2.0 * S5_GROUP) ** -0.5),
        "s5_c_re": nrm(ks[16], (L, G, S5_GROUP, P), (2.0 * P) ** -0.5),
        "s5_c_im": nrm(ks[17], (L, G, S5_GROUP, P), (2.0 * P) ** -0.5),
        "s5_d": nrm(ks[18], (L, W), 1.0),
        "s5_glu_w": nrm(ks[19], (L, W, W), W ** -0.5),
        "s5_glu_b": nrm(ks[20], (L, W), 0.02),
        "w_branch": nrm(ks[21], (L, N_BRANCH, W, D), W ** -0.5),
        "w_out": nrm(ks[22], (L, D, D), D ** -0.5),
    }

def reference(x, c, positions, ada_w, ada_b, norm_g, w_in, hg_lb_logits, hg_onorm_g,
              at_qnorm_g, at_knorm_g, s5_a_re, s5_a_im, s5_log_dt, s5_b_re, s5_b_im,
              s5_c_re, s5_c_im, s5_d, s5_glu_w, s5_glu_b, w_branch, w_out):
    p = jax.nn.softmax(hg_lb_logits.astype(jnp.float32), axis=0)
    lb_all = jnp.cumsum(p, axis=0) - p[0:1]
    for l in range(DEPTH):
        x = hybrid_layer(x, c, lb_all[l], ada_w[l], ada_b[l], norm_g[l], w_in[l], hg_onorm_g[l],
                         at_qnorm_g[l], at_knorm_g[l], s5_a_re[l], s5_a_im[l], s5_log_dt[l],
                         s5_b_re[l], s5_b_im[l], s5_c_re[l], s5_c_im[l], s5_d[l],
                         s5_glu_w[l], s5_glu_b[l], w_branch[l], w_out[l], positions)
    return x


_drawn_inputs = setup_inputs


def setup_inputs(seed=0):
    import zlib

    import numpy as np

    out = dict(_drawn_inputs(seed))
    spreads = {}
    factors = {'ada_b': 3.398,
     'norm_g': 8.0,
     'hg_lb_logits': 6.075,
     'hg_onorm_g': 8.0,
     'at_qnorm_g': 8.0,
     'at_knorm_g': 8.0,
     's5_a_re': 64.0,
     's5_a_im': 64.0,
     's5_log_dt': 64.0,
     's5_b_re': 64.0,
     's5_b_im': 64.0,
     's5_c_re': 64.0,
     's5_c_im': 64.0,
     's5_glu_w': 2.673,
     's5_glu_b': 8.0}
    for name, (base, spread) in spreads.items():
        noise = np.random.default_rng([zlib.crc32(name.encode()), seed]).standard_normal(out[name].shape)
        drawn = base * np.exp(spread * noise) if base else spread * noise
        out[name] = __import__('jax').numpy.asarray(drawn.astype(out[name].dtype))
    for name, factor in factors.items():
        out[name] = (out[name] * factor).astype(out[name].dtype)
    return out
```

```python
import math
from contextlib import ExitStack

import numpy as np
import concourse.bass as bass
from concourse import mybir

F32 = mybir.dt.float32
F32R = mybir.dt.float32r
I32 = mybir.dt.int32
ALU = mybir.AluOpType
ACT = mybir.ActivationFunctionType
AX = mybir.AxisListType

P = 128
DEPTH, S, D, W = 2, 512, 1024, 512
ND = D // P
NT = S // P
NW = W // P
HEADS, HD = 4, 128
IH, IDIM = 8, 64
TOPK = 128
EPS = 1e-6
NEG_BIG = -1e30
TAKEN = -3e38
LEVELS = [1, 2, 4, 8, 16, 32, 64]
G, GC, SP_ = 32, 16, 64
QG = P // GC
CH = 8
NCH = S // CH
KC, NCOL = 4, 256
CHUNK = KC * NCOL
RAW_SLOTS, SPLIT_SLOTS = 4, 3
ATT_SCALE = 1.0 / math.sqrt(HD)
MAGIC = 12582912.0
INV2PI = 0.15915494309189535
PI_A, PI_B, PI_C = 6.28125, 0.0019350051879882812, 3.0199159819567018e-07
PI_IN = 3.1415925
HALF_PI = math.pi / 2

COLS = {"hq": (0, 512), "hf": (512, 512), "hv": (1024, 512), "hg": (1536, 512), "q": (2048, 512),
        "kv": (2560, 256), "ag": (2816, 512), "iq": (3328, 512), "ikw": (3840, 72),
        "su": (3912, 512), "sg": (4424, 512), "mg": (4936, 3072)}
IKW = 72


def schedule():
    steps = [("xT", k) for k in range(ND)]
    steps += [("ada", 0, c) for c in range(24)]
    for l in range(DEPTH):
        todo = [("ada", l + 1, c) for c in range(24)] if l + 1 < DEPTH else []

        def more(n):
            out = todo[:n]
            del todo[:n]
            return out

        steps += [("h", l)]
        steps += [("tm", l, "iq"), ("tm", l, "ikw"), ("ikT", l), ("tm", l, "kv")]
        steps += [("iqT", l, t) for t in range(1, NT)]
        steps += [("tm", l, "q"), ("kT", l)] + [("idx", l, 3, h) for h in range(IH)] + [("topk", l, 3)]
        steps += [("tm", l, "hv")] + [("qT", l, t) for t in range(NT)]
        for p in range(2):
            steps += [("cm", l, "hf", p), ("cm", l, "hq", p)]
            steps += [("hg", l, p)]
            steps += [("cm", l, "hg", p)]
            b = 2 - p
            steps += [("idx", l, b, h) for h in range(IH)] + [("topk", l, b)] + more(2)
        steps += [("cm", l, "su", p) for p in range(2)] + [("s5u", l)]
        for j in range(4):
            steps += [("cm", l, "mg0", j), ("cm", l, "wb0", j)] + more(3)
            steps += [("att", l, j)]
        for p in range(2):
            steps += [("cm", l, "ag", p)]
        for j in range(4):
            steps += [("cm", l, "mg1", j), ("cm", l, "wb1", j)] + more(3)
            steps += [("s5", l, j)]
        steps += [("gelu", l)]
        steps += [("cm", l, "glu", p) for p in range(2)]
        steps += [("cm", l, "sg", p) for p in range(2)]
        for j in range(4):
            steps += [("cm", l, "mg2", j), ("cm", l, "wb2", j)] + more(3)
        steps += [("msplit", l)]
        for j in range(4):
            steps += [("cm", l, "wo", j)]
            if l == DEPTH - 1 and j % 2:
                steps += [("outT", j // 2, t) for t in range(NT)]
        assert not todo
    return steps


def chunks_of(step):
    kind = step[0]
    if kind == "ada":
        _, l, c = step
        return [("ada_w", l, KC * (c % 2), NCOL * (c // 2), NCOL)]
    if kind == "tm":
        _, l, name = step
        col, width = COLS[name]
        return [("w_in", l, KC * kh, col + c0, min(NCOL, width - c0))
                for c0 in range(0, width, NCOL) for kh in range(2)]
    if kind == "cm":
        _, l, name, j = step
        if name[:2] == "wb":
            return [(name, l, 0, NCOL * j, NCOL)]
        if name == "glu":
            return [("s5_glu_w", l, 0, NCOL * j, NCOL)]
        if name == "wo":
            return [("w_out", l, KC * kh, NCOL * j, NCOL) for kh in range(2)]
        col = COLS["mg"][0] + D * int(name[2]) if name[:2] == "mg" else COLS[name][0]
        return [("w_in", l, KC * kh, col + NCOL * j, NCOL) for kh in range(2)]
    return []


STEPS = schedule()
CHUNKS = [(c, step[0] == "ada") for step in STEPS for c in chunks_of(step)]
FULL = [n for n, (c, _) in enumerate(CHUNKS) if c[4] == NCOL]
NARROW = [n for n, (c, _) in enumerate(CHUNKS) if c[4] != NCOL]


def first_chunks():
    first, n = {}, 0
    for step in STEPS:
        first[step] = n
        n += len(chunks_of(step))
    return first


FIRST = first_chunks()


class Banks:

    def __init__(self):
        self.uses, self.full = {}, {}
        count, done = [0] * 8, [0] * 8
        pair, ring = 0, 0
        for step in STEPS:
            kind = step[0]
            if kind == "tm":
                got = [((step, t), t, True) for t in range(NT)]
            elif kind == "cm":
                got = [((step, i), 2 * pair + i, True) for i in range(2)]
                pair ^= 1
            elif kind == "ada":
                got = [(("ada", step[1]), 7, True)] if step[2] == 0 else []
            elif kind == "h":
                got = [((step, 0), 7, False)]
            else:
                got = []
                if kind == "hg":
                    got = [((step, n), bank, False) for n, bank in enumerate(HG_BANKS)]
                for n in range(BANKS_OF[kind](step) if kind in BANKS_OF else 0):
                    got.append(((step, n), 4 + ring, False))
                    ring = (ring + 1) % 3
            for key, bank, by_chunk in got:
                self.uses[key] = (bank, count[bank])
                count[bank] += 1
                if by_chunk:
                    last = FIRST[step] + len(chunks_of(step)) - 1 if kind != "ada" else FIRST[("ada", step[1], 23)]
                    self.full[key] = ("chunk", last + 1)
                else:
                    done[bank] += 1
                    self.full[key] = (bank, done[bank])


BANKS_OF = {
    "xT": lambda s: 1, "ikT": lambda s: 1, "iqT": lambda s: 1, "kT": lambda s: 1, "qT": lambda s: 1,
    "idx": lambda s: 1,
    "att": lambda s: HEADS + (s[2] + 1) + 1,
    "s5": lambda s: 2 + 2 + 2 + 1,
    "outT": lambda s: 1,
}
HG_LEV, HG_KT, HG_O, HG_ST, HG_SS = 0, 16, 18, 20, 26
HG_BANKS = [4 + n % 3 for n in range(16)] + [5, 6] + [4, 5] + [6, 0] * 3 + [6, 0]
BANKS = Banks()


VEC_COLS = 24 + 8 + 1 + 4 + 4
V_ADAB, V_NORM, V_ONORM, V_D, V_GLUB = 0, 24, 32, 33, 37
CONST_COLS = 1164
HG0 = 11936
ARENA = HG0 + 9984
NPOW = CH + 1


def split_of():
    out, n = {}, 0
    for i, (_, is_ada) in enumerate(CHUNKS):
        if not is_ada:
            out[i] = n
            n += 1
    return out


SPLIT_NO = split_of()
SPLIT_CHUNK = sorted(SPLIT_NO)


def program(nc, wfull, wnarrow, x, cvec, pos, lblog, vecs, gains, s5v, s5m, consts, masks, out):
    x_scratch = nc.dram_tensor("x_scratch", (DEPTH, P, ND, S), F32, kind="Internal").ap()
    u_scratch = nc.dram_tensor("u_scratch", (DEPTH, NW, P, CH, NCH), F32, kind="Internal").ap()
    y_scratch = nc.dram_tensor("y_scratch", (DEPTH, NW, P, QG, NCH), F32, kind="Internal").ap()

    with ExitStack() as ctx:
        def sb(name, shape, dt=F32):
            return ctx.enter_context(nc.sbuf_tensor(name, shape, dt))

        def sem(name):
            return ctx.enter_context(nc.semaphore(name))

        raw = sb("raw", [P, RAW_SLOTS, KC, NCOL])
        w_hi = sb("w_hi", [P, SPLIT_SLOTS, KC, NCOL], F32R)
        w_lo = sb("w_lo", [P, SPLIT_SLOTS, KC, NCOL], F32R)
        xm = sb("xm", [P, ND, S])
        h_hi = sb("h_hi", [P, ND, S], F32R)
        h_lo = sb("h_lo", [P, ND, S], F32R)
        y_hi = sb("y_hi", [P, NW, S], F32R)
        y_lo = sb("y_lo", [P, NW, S], F32R)
        cst = sb("cst", [P, CONST_COLS])
        msk = sb("msk", [P, len(LEVELS), P])
        sig = sb("sig", [P, 2, S])
        prod = sb("prod", [P, 2, S])
        cos_t = sb("cos_t", [P, NT, 64])
        sin_t = sb("sin_t", [P, NT, 64])
        vec = sb("vec", [P, DEPTH, VEC_COLS])
        gq = sb("gq", [P, DEPTH, 2, HD])
        s5p = sb("s5p", [P, DEPTH, 3, G])
        cs = sb("cs", [P, 3, ND])
        posi = sb("posi", [P, NT], I32)
        posf = sb("posf", [P, NT])
        lbt = sb("lbt", [P, 8, NW])
        lb = sb("lb", [P, DEPTH, 2, NW])
        mod = sb("mod", [P, DEPTH, 24])
        stat = sb("stat", [P, 64])
        s5s = sb("s5s", [P, 14, G])
        arena = sb("arena", [P, ARENA])

        def region(at, *shape):
            size = int(np.prod(shape))
            view = arena[:, at:at + size]
            if len(shape) > 1:
                names = "abcd"[:len(shape)]
                view = view.rearrange(f"p ({' '.join(names)}) -> p {' '.join(names)}",
                                      **dict(zip(names[1:], shape[1:])))
            return view

        tmb = region(0, NT, S)
        logit = region(0, HEADS, S)
        iq_t = region(2048, NT, S)
        o_att = region(2048, HEADS, S)
        q_t = region(4096, HEADS, S)
        kv = region(6144, NT, 256)
        k_t = region(7168, S)
        ikd = region(7680, NT, 136)
        ik_t = region(8224, S)
        isc = region(8736, 1152)
        rope = region(8736, 2, S)
        p_t = region(9888, NT, S)
        rl = region(9888, 2, S)
        work = region(10912, S)
        hv = region(HG0, NT, S)
        lf = region(HG0 + 2048, 2, S)
        hq = region(HG0 + 3072, 2, S)
        hk = region(HG0 + 4096, 2, S)
        dd = region(HG0 + 5120, 2, S)
        kdt = region(HG0 + 5120, 2, 4, P)
        qp = region(HG0 + 6144, 2, S)
        kp = region(HG0 + 7168, 2, S)
        sct = region(HG0 + 8192, 2, S)
        st = region(HG0 + 9216, 2, 3, P)
        sq = region(0, 2, S)
        rb = region(1024, S)
        ht = region(1536, 4, S)
        x_tm = region(4096, NT, D)
        up = region(HG0, NW, S)
        par = region(HG0 + 2048, 4, G, GC)
        y_cm = region(HG0 + 4096, NW, S)
        y_g = region(HG0 + 6144, NW, S)
        bbs = region(HG0 + 8192, 2, QG, GC)
        cct = region(HG0 + 8448, 2, QG, GC)
        m8 = region(HG0 + 8704, QG, NCH)
        pw = region(HG0 + 9216, 2, NPOW, G)
        pwt = region(0, 3, NPOW, G)
        wmat = region(0, QG, P)
        wtmp = region(1024, QG, NPOW, GC)
        ca1 = region(2176, QG, NPOW, GC)
        ca2 = region(3328, QG, CH, GC)
        wt1 = region(4352, QG, P)
        wt2 = region(5376, QG, P)
        kt = region(6400, QG, P)
        mt = region(7424, QG, P)
        tang = region(1024, QG, NCH)
        tcos = region(8448, QG, NCH)
        tsin = region(8960, QG, NCH)
        u_j = region(9472, QG, NCH)
        zz = region(9984, QG, NCH)
        tt = region(10496, QG, NCH)
        v2 = region(11008, QG, NCH)
        x_back = region(0, ND, S)
        o_tm = region(4096, NT, D)

        bank = [ctx.enter_context(nc.psum_tensor(f"bank{n}", [P, S], F32)) for n in range(8)]

        ident, ones, reset = cst[:, 0:128], cst[:, 128:256], cst[:, 256:768]
        invf, nidx = cst[:, 768:832], cst[:, 832:896]
        cmin, cneg, sgn, mpow = cst[:, 896:1024], cst[:, 1024:1152], cst[:, 1152:1153], cst[:, 1153:1162]
        half_pi, eps = cst[:, 1162:1163], cst[:, 1163:1164]

        bank_full = [sem(f"bank{n}_full") for n in range(8)]
        bank_read = [sem(f"bank{n}_read") for n in range(8)]
        chunk_done = sem("chunk_done")
        raw_full = [sem(f"raw{n}_full") for n in range(RAW_SLOTS)]
        hi_done, lo_done = sem("hi_done"), sem("lo_done")
        const_in, x_in = sem("const_in"), sem("x_in")
        dve_step, act_step = sem("dve_step"), sem("act_step")
        cs_sig, cs_ready = sem("cs_sig"), sem("cs_ready")
        lb_exp, ang_ready, rope_tab = sem("lb_exp"), sem("ang_ready"), sem("rope_tab")
        mod_ready = sem("mod_ready")
        sq_ready, r_ready, t_ready, hhi_done, h_ready = (
            sem("sq_ready"), sem("r_ready"), sem("t_ready"), sem("hhi_done"), sem("h_ready"))
        tm_roped = sem("tm_roped")
        ssq_ready, rstd_ready = sem("ssq_ready"), sem("rstd_ready")
        rl_ready, rl_used, mask_ready = sem("rl_ready"), sem("rl_used"), sem("mask_ready")
        neg_ready, exp_ready, p_ready = sem("neg_ready"), sem("exp_ready"), sem("p_ready")
        hf_sig, hf_ready, lf_ready, b_ready = sem("hf_sig"), sem("hf_ready"), sem("lf_ready"), sem("b_ready")
        d_ready, e_ready, qk_ready = sem("d_ready"), sem("e_ready"), sem("qk_ready")
        st_ready, hsq_ready, hr_ready, ya_ready = sem("st_ready"), sem("hsq_ready"), sem("hr_ready"), sem("ya_ready")
        sig_ready, prod_ready, y_hi_done, y_done = (
            sem("sig_ready"), sem("prod_ready"), sem("y_hi_done"), sem("y_done"))
        merged, m_hi_done, m_done = sem("merged"), sem("m_hi_done"), sem("m_done")
        x_saved, x_back_in, out_saved = sem("x_saved"), sem("x_back_in"), sem("out_saved")
        sq_used, glu_used, gl_lo, s5_dt, s5_pow = (
            sem("sq_used"), sem("glu_used"), sem("gl_lo"), sem("s5_dt"), sem("s5_pow"))
        up_ready, u_saved, u_in, par_in = sem("up_ready"), sem("u_saved"), sem("u_in"), sem("par_in")
        s5_ang, s5_trig, s5_w, s5_tab_ang, s5_tab = (
            sem("s5_ang"), sem("s5_trig"), sem("s5_w"), sem("s5_tab_ang"), sem("s5_tab"))
        kt_ready, mt_in, mt_clear, v_ready = sem("kt_ready"), sem("mt_in"), sem("mt_clear"), sem("v_ready")
        ysb_ready, y_saved, ycm_in = sem("ysb_ready"), sem("y_saved"), sem("ycm_in")
        gl_sq, gl_arg, gl_sig, gl_split, gl_hi = (
            sem("gl_sq"), sem("gl_arg"), sem("gl_sig"), sem("gl_split"), sem("gl_hi"))
        glu_sig = sem("glu_sig")

        def wait_free(e, key):
            b, u = BANKS.uses[key]
            if u:
                e.wait_ge(bank_read[b], u)
            return bank[b]

        def wait_full(e, key):
            b, _ = BANKS.uses[key]
            where, value = BANKS.full[key]
            e.wait_ge(chunk_done if where == "chunk" else bank_full[where], value)
            return bank[b]

        def wait_read(e, key):
            b, u = BANKS.uses[key]
            e.wait_ge(bank_read[b], u + 1)

        def full(key):
            return bank_full[BANKS.uses[key][0]]

        def read(key):
            return bank_read[BANKS.uses[key][0]]

        block = ctx.enter_context(nc.Block())

        def wait_x(e, l, k):
            wait_read(e, (("xT", k), 0) if l == 0 else (("cm", l - 1, "wo", k // 2), k % 2))

        def gate_no(l, branch, i):
            return 12 * l + 4 * branch + i

        def sig_no(l, what, i):
            at = {"hg": 0, "mg0": 4, "ag": 12, "mg1": 16, "sg": 24, "mg2": 28}
            return 36 * l + at[what] + i

        def idx_no(l, b, h):
            return IH * (3 * l + 3 - b) + h

        def d_no(l, p, n):
            return 16 * (2 * l + p) + n

        def e_no(l, p, n):
            return 18 * (2 * l + p) + n

        def mrg_no(l, branch, k):
            return 2 * ND * l + ND * (branch - 1) + k

        SIGS = []
        for l in range(DEPTH):
            for name in ("hg", "mg0", "ag", "mg1", "sg", "mg2"):
                for j in range(2 if name[0] != "m" else 4):
                    SIGS += [(("cm", l, name if name[0] != "m" else "wb" + name[2], j), i) for i in range(2)]

        def y_unused(e, l, what):
            last = {"hg": ("cm", l - 1, "wb2", 3), "ag": ("cm", l, "wb0", 3), "gelu": ("cm", l, "wb1", 3),
                    "sg": ("cm", l, "glu", 1)}[what]
            if last in FIRST:
                e.wait_ge(chunk_done, FIRST[last] + len(chunks_of(last)))

        ISC = {1: 0, 2: 256, 3: 640}
        ATT_LAST = [("att", l, NT - 1) for l in range(DEPTH)]

        @block.sync
        def _(sp):
            for a, b in ((cst, consts), (msk, masks), (vec, vecs), (gq, gains), (s5p, s5v), (posi, pos),
                         (lbt[:, 0:DEPTH], lblog), (cs[:, 0], cvec)):
                sp.dma_start(a[:] if not isinstance(a, bass.AP) else a, b).then_inc(const_in, 16)
            for t in range(NT):
                sp.dma_start(x_tm[:, t], x[t * P:(t + 1) * P, :]).then_inc(x_in, 16)
            sent = 0
            full_no = {n: i for i, n in enumerate(FULL)}
            narrow_no = {n: i for i, n in enumerate(NARROW)}
            for step in STEPS:
                upto = min(len(CHUNKS), FIRST[step] + len(chunks_of(step)) + RAW_SLOTS - 1)
                for n in range(sent, upto):
                    slot = n % RAW_SLOTS
                    if n >= RAW_SLOTS:
                        old = n - RAW_SLOTS
                        if old in SPLIT_NO:
                            sp.wait_ge(lo_done, SPLIT_NO[old] + 1)
                        else:
                            sp.wait_ge(chunk_done, old + 1)
                    if n in full_no:
                        sp.dma_start(raw[:, slot], wfull[full_no[n]]).then_inc(raw_full[slot], 16)
                    else:
                        sp.dma_start(raw[:, slot, :, 0:IKW], wnarrow[narrow_no[n]]).then_inc(raw_full[slot], 16)
                sent = max(sent, upto)
                kind, l = step[0], step[1]
                if kind == "tm" and step[2] == "iq":
                    for k in range(ND):
                        wait_x(sp, l, k)
                    sp.dma_start(x_scratch[l], xm[:]).then_inc(x_saved, 16)
                if kind == "s5u":
                    sp.wait_ge(y_done, gate_no(l, 0, 3) + 1)
                    sp.dma_start(par, s5m[l]).then_inc(par_in, 16)
                if kind == "cm" and step[2] == "wb0" and step[3] == 0:
                    sp.wait_ge(u_saved, 16 * (l + 1))
                if kind == "s5":
                    j = step[2]
                    if j == 0:
                        wait_read(sp, (ATT_LAST[l], 2 * HEADS))
                    else:
                        wait_read(sp, (("s5", l, j - 1), 6))
                    for jj in range(CH):
                        sp.dma_start(u_j[jj * GC:(jj + 1) * GC], u_scratch[l, j, :, jj, :].rearrange(
                            "(g c) n -> c g n", g=QG)).then_inc(u_in, 16)
                    wait_read(sp, (step, 0))
                    wait_read(sp, (step, 1))
                    sp.wait_ge(mt_clear, l + 1)
                    for jj in range(CH):
                        sp.dma_start(mt[jj * GC:(jj + 1) * GC, :, jj * GC:P],
                                     kt[0:GC, :, 0:(CH - jj) * GC]).then_inc(mt_in, 16)
                    wait_read(sp, (step, 6))
                    sp.dma_start(y_scratch[l, j], tt).then_inc(y_saved, 16)
                    sp.wait_ge(y_saved, 16 * (NW * l + j + 1))
                    for gg in range(QG):
                        sp.dma_start(y_cm[gg * GC:(gg + 1) * GC, j].rearrange("p (j n) -> p j n", j=CH),
                                     y_scratch[l, j, :, gg, :].rearrange("(j c) n -> c j n", j=CH)
                                     ).then_inc(ycm_in, 16)
                if kind == "cm" and step[2] == "glu" and step[3] == 1:
                    sp.wait_ge(ycm_in, 16 * QG * NW * (l + 1))
                    sp.dma_start(x_back, x_scratch[l]).then_inc(x_back_in, 16)
                if kind == "outT":
                    half, t = step[1], step[2]
                    wait_read(sp, (step, 0))
                    sp.dma_start(out[t * P:(t + 1) * P, half * S:(half + 1) * S],
                                 o_tm[:, t, half * S:(half + 1) * S]).then_inc(out_saved, 16)
            sp.wait_ge(out_saved, 16 * 2 * NT)
            sp.wait_ge(x_saved, 16 * DEPTH)
            sp.wait_ge(y_saved, 16 * NW * DEPTH)

        @block.gpsimd
        def _(pool):
            for m, n in enumerate(SPLIT_CHUNK):
                width = CHUNKS[n][0][4]
                pool.wait_ge(hi_done, m + 1)
                hi, lo = w_hi[:, m % SPLIT_SLOTS, :, 0:width], w_lo[:, m % SPLIT_SLOTS, :, 0:width]
                nc.gpsimd.tensor_tensor(lo, raw[:, n % RAW_SLOTS, :, 0:width], hi.bitcast(F32),
                                        ALU.subtract).then_inc(lo_done, 1)

        @block.scalar
        def _(act):
            steps = [0]

            def then_wait(ins):
                steps[0] += 1
                ins.then_inc(act_step, 1)
                act.wait_ge(act_step, steps[0])

            hi = [0]

            def high_parts(upto):
                while hi[0] < len(SPLIT_CHUNK) and SPLIT_CHUNK[hi[0]] < upto:
                    m = hi[0]
                    n = SPLIT_CHUNK[m]
                    width = CHUNKS[n][0][4]
                    act.wait_ge(raw_full[n % RAW_SLOTS], 16 * (n // RAW_SLOTS + 1))
                    if m >= SPLIT_SLOTS:
                        act.wait_ge(chunk_done, SPLIT_CHUNK[m - SPLIT_SLOTS] + 1)
                    nc.scalar.activation(w_hi[:, m % SPLIT_SLOTS, :, 0:width],
                                         raw[:, n % RAW_SLOTS, :, 0:width], ACT.Copy).then_inc(hi_done, 1)
                    hi[0] += 1

            act.wait_ge(const_in, 16 * 8)
            nc.scalar.activation(cs[:, 1], cs[:, 0], ACT.Sigmoid).then_inc(cs_sig, 1)
            act.wait_ge(ang_ready, 1)
            nc.scalar.activation(sin_t[:], sin_t[:], ACT.Sin).then_inc(rope_tab, 1)
            then_wait(nc.scalar.activation(cos_t[:], cos_t[:], ACT.Sin, scale=-1.0, bias=half_pi))
            act.wait_ge(lb_exp, 1)
            nc.scalar.activation(lbt[:, 2:2 + DEPTH], lbt[:, 2:2 + DEPTH], ACT.Exp).then_inc(rope_tab, 1)

            for step in STEPS:
                kind, l = step[0], step[1]
                high_parts(FIRST[step] + len(chunks_of(step)) + 2)
                if kind == "xT":
                    src = wait_full(act, (step, 0))
                    nc.scalar.activation(xm[:, step[1]], src[:], ACT.Copy).then_inc(read((step, 0)), 1)
                if kind == "h":
                    for k in range(ND):
                        wait_x(act, l, k)
                        if k >= 2:
                            act.wait_ge(sq_used, (ND - 1) * l + k - 1)
                        nc.scalar.activation(sq[:, k % 2], xm[:, k], ACT.Square).then_inc(sq_ready, 1)
                    src = wait_full(act, (step, 0))
                    nc.scalar.activation(rb, src[:], ACT.Ln, scale=1.0 / D, bias=eps).then_inc(read((step, 0)), 1)
                    wait_read(act, (step, 0))
                    nc.scalar.activation(rb, rb, ACT.Exp, scale=-0.5).then_inc(r_ready, 1)
                    if l:
                        act.wait_ge(chunk_done, FIRST[step])
                    for k in range(ND):
                        act.wait_ge(t_ready, ND * l + k + 1)
                        nc.scalar.activation(h_hi[:, k], ht[:, k % 4], ACT.Identity,
                                             bias=mod[:, l, k:k + 1]).then_inc(hhi_done, 1)
                if kind == "tm":
                    name = step[2]
                    if name == "q":
                        for t in range(1, NT):
                            wait_full(act, (("iqT", l, t), 0))
                    for t in range(NT):
                        src = wait_full(act, (step, t))
                        if name == "ikw":
                            nc.scalar.activation(ikd[:, t, 0:64], src[:, 0:64], ACT.Copy)
                            nc.scalar.activation(ikd[:, t, 64:136], src[:, 0:72], ACT.Copy).then_inc(read((step, t)), 1)
                        else:
                            dst, wd = {"iq": (tmb, S), "q": (tmb, S), "kv": (kv, 256), "hv": (hv, S)}[name]
                            nc.scalar.activation(dst[:, t], src[:, 0:wd], ACT.Copy).then_inc(read((step, t)), 1)
                    if name == "q":
                        act.wait_ge(ssq_ready, l + 1)
                        then_wait(nc.scalar.activation(stat[:, 0:20], stat[:, 0:20], ACT.Ln, scale=1.0 / HD,
                                                       bias=eps))
                        nc.scalar.activation(stat[:, 0:20], stat[:, 0:20], ACT.Exp, scale=-0.5).then_inc(rstd_ready, 1)
                if kind in ("ikT", "kT"):
                    src = wait_full(act, (step, 0))
                    nc.scalar.activation(ik_t if kind == "ikT" else k_t, src[:], ACT.Copy).then_inc(read((step, 0)), 1)
                if kind in ("iqT", "qT"):
                    t = step[2]
                    src = wait_full(act, (step, 0))
                    nc.scalar.activation((iq_t if kind == "iqT" else q_t)[:, :, t * P:(t + 1) * P],
                                         src[:].rearrange("p (a b) -> p a b", a=NT), ACT.Copy
                                         ).then_inc(read((step, 0)), 1)
                if kind == "idx":
                    _, _, b, h = step
                    n = idx_no(l, b, h)
                    src = wait_full(act, (step, 0))
                    if n >= 2:
                        act.wait_ge(rl_used, n - 1)
                    nc.scalar.activation(rl[:, n % 2, 0:(b + 1) * P], src[:, 0:(b + 1) * P], ACT.Relu
                                         ).then_inc(read((step, 0)), 1)
                if kind == "att":
                    b = step[2]
                    act.wait_ge(neg_ready, NT * l + b + 1)
                    for h in range(HEADS):
                        nc.scalar.activation(logit[:, h, 0:(b + 1) * P], logit[:, h, 0:(b + 1) * P], ACT.Exp,
                                             bias=stat[:, 32 + h:33 + h], accum_out=stat[:, 36 + h:37 + h]
                                             ).then_inc(exp_ready, 1)
                    for kt_no in range(b + 1):
                        src = wait_full(act, (step, HEADS + kt_no))
                        nc.scalar.activation(p_t[:, kt_no], src[:], ACT.Copy).then_inc(read((step, HEADS + kt_no)), 1)
                    src = wait_full(act, (step, HEADS + b + 1))
                    nc.scalar.activation(o_att[:, :, b * P:(b + 1) * P], src[:].rearrange("p (a b) -> p a b", a=HEADS),
                                         ACT.Copy).then_inc(read((step, HEADS + b + 1)), 1)
                if kind == "cm" and step[2] == "hf":
                    if step[3]:
                        act.wait_ge(prod_ready, gate_no(l, 0, 1) + 1)
                    for i in range(2):
                        src = wait_full(act, (step, i))
                        nc.scalar.activation(lf[:, i], src[:], ACT.Sigmoid).then_inc(read((step, i)), 1)
                    for i in range(2):
                        act.wait_ge(hf_ready, 4 * l + 2 * step[3] + i + 1)
                        nc.scalar.activation(lf[:, i], lf[:, i], ACT.Ln).then_inc(lf_ready, 1)
                if kind == "cm" and step[2] == "hq":
                    for i in range(2):
                        src = wait_full(act, (step, i))
                        nc.scalar.activation(hq[:, i], src[:], ACT.Copy).then_inc(read((step, i)), 1)
                if kind == "hg":
                    p = step[2]
                    for n in range(2 * len(LEVELS)):
                        m, i = LEVELS[n // 2], n % 2
                        act.wait_ge(d_ready, d_no(l, p, n) + 1)
                        view = dd[:, i].rearrange("p (n m) -> p n m", m=2 * m)
                        nc.scalar.activation(view[:, :, 0:m], view[:, :, 0:m], ACT.Exp, scale=-1.0)
                        nc.scalar.activation(view[:, :, m:2 * m], view[:, :, m:2 * m], ACT.Exp).then_inc(e_ready, 1)
                    for i in range(2):
                        act.wait_ge(d_ready, d_no(l, p, 14 + i) + 1)
                        nc.scalar.activation(dd[:, i], dd[:, i], ACT.Exp, scale=-1.0).then_inc(e_ready, 1)
                        nc.scalar.activation(lf[:, i], lf[:, i], ACT.Exp).then_inc(e_ready, 1)
                    for i in range(2):
                        src = wait_full(act, (step, HG_KT + i))
                        nc.scalar.activation(kdt[:, i, 0:3], src[:, 0:3 * P].rearrange("p (a b) -> p a b", a=3), ACT.Copy
                                             ).then_inc(read((step, HG_KT + i)), 1)
                    for i in range(2):
                        src = wait_full(act, (step, HG_O + i))
                        nc.scalar.activation(hk[:, i], src[:], ACT.Square).then_inc(hsq_ready, 1)
                    for i in range(2):
                        src = wait_full(act, (step, HG_SS + i))
                        nc.scalar.activation(dd[:, i], src[:], ACT.Ln, scale=1.0 / HD, bias=eps
                                             ).then_inc(read((step, HG_SS + i)), 1)
                        wait_read(act, (step, HG_SS + i))
                        nc.scalar.activation(dd[:, i], dd[:, i], ACT.Exp, scale=-0.5).then_inc(hr_ready, 1)
                if kind == "cm" and step[2] in ("hg", "ag", "sg", "mg0", "mg1", "mg2"):
                    name, j = step[2], step[3]
                    for i in range(2):
                        src = wait_full(act, (step, i))
                        n = sig_no(l, name, 2 * j + i)
                        if n >= 2:
                            wait_read(act, SIGS[n - 2])
                        nc.scalar.activation(sig[:, n % 2], src[:], ACT.Sigmoid).then_inc(
                            read((step, i)) if name[0] == "m" else sig_ready, 1)
                    if name[0] != "m":
                        branch = {"hg": 0, "ag": 1, "sg": 2}[name]
                        for i in range(2):
                            n = gate_no(l, branch, 2 * j + i)
                            act.wait_ge(prod_ready, n + 1)
                            if i == 0 and j == 0:
                                y_unused(act, l, name)
                            nc.scalar.activation(y_hi[:, 2 * j + i], prod[:, n % 2], ACT.Copy).then_inc(y_hi_done, 1)
                if kind == "cm" and step[2] == "su":
                    for i in range(2):
                        src = wait_full(act, (step, i))
                        if step[3] == 0 and i == 0:
                            act.wait_ge(y_done, gate_no(l, 0, 3) + 1)
                        nc.scalar.activation(up[:, 2 * step[3] + i].rearrange("p (j n) -> p j n", j=CH),
                                             src[:].rearrange("p (n j) -> p j n", j=CH), ACT.Copy
                                             ).then_inc(read((step, i)), 1)
                if kind == "s5u":
                    wait_read(act, (("cm", l, "su", 1), 1))
                    act.dma_start(u_scratch[l].rearrange("q p j n -> p q (j n)"), up).then_inc(u_saved, 16)
                if kind == "s5":
                    j = step[2]
                    if j == 0:
                        wait_read(act, (ATT_LAST[l], 2 * HEADS))
                        nc.scalar.activation(s5s[:, 0], s5p[:, l, 2], ACT.Exp).then_inc(s5_dt, 1)
                        act.wait_ge(s5_ang, l + 1)
                        nc.scalar.activation(pwt[:, 1], pwt[:, 1], ACT.Exp)
                        nc.scalar.activation(pw[:, 1], pwt[:, 0], ACT.Sin)
                        nc.scalar.activation(pw[:, 0], pwt[:, 2], ACT.Sin, scale=-1.0, bias=half_pi
                                             ).then_inc(s5_trig, 1)
                    act.wait_ge(s5_tab_ang, NW * l + j + 1)
                    nc.scalar.activation(tsin, tang, ACT.Sin)
                    nc.scalar.activation(tcos, tcos, ACT.Sin, scale=-1.0, bias=half_pi).then_inc(s5_tab, 1)
                    for q in range(2):
                        src = wait_full(act, (step, q))
                        if q == 0 and (l or j):
                            act.wait_ge(mt_in, 16 * CH * (NW * l + j))
                        nc.scalar.activation(kt[0:GC, 4 * q:4 * q + 4], src[0:GC].rearrange("p (a b) -> p a b", a=4),
                                             ACT.Copy).then_inc(read((step, q)), 1)
                    for q in range(2):
                        src = wait_full(act, (step, 2 + q))[:].rearrange("p (a b) -> p a b", a=4)
                        gs = slice(4 * q, 4 * q + 4)
                        nc.scalar.activation(wt1[:, gs], src, ACT.Copy)
                        nc.scalar.activation(wt2[:, gs, 0:SP_], src[:, :, SP_:P], ACT.Copy)
                        nc.scalar.activation(wt2[:, gs, SP_:P], src[:, :, 0:SP_], ACT.Copy, scale=-1.0
                                             ).then_inc(read((step, 2 + q)), 1)
                    src = wait_full(act, (step, 6))
                    nc.scalar.activation(tt, src[:].rearrange("p (g n) -> p g n", g=QG), ACT.Copy
                                         ).then_inc(read((step, 6)), 1)
                if kind == "gelu":
                    for k in range(NW):
                        act.wait_ge(gl_sq, NW * l + k + 1)
                        if k == 0:
                            y_unused(act, l, "gelu")
                        nc.scalar.activation(prod[:, k % 2], y_g[:, k], ACT.Square).then_inc(gl_arg, 1)
                        act.wait_ge(gl_sig, NW * l + k + 1)
                        nc.scalar.activation(prod[:, k % 2], prod[:, k % 2], ACT.Sigmoid,
                                             scale=2 * math.sqrt(2 / math.pi)).then_inc(gl_arg, 1)
                        act.wait_ge(gl_split, NW * l + k + 1)
                        nc.scalar.activation(y_hi[:, k], y_g[:, k], ACT.Copy).then_inc(gl_hi, 1)
                if kind == "cm" and step[2] == "glu":
                    for i in range(2):
                        k = 2 * step[3] + i
                        src = wait_full(act, (step, i))
                        if k >= 2:
                            act.wait_ge(glu_used, NW * l + k - 1)
                        nc.scalar.activation(prod[:, k % 2], src[:], ACT.Sigmoid,
                                             bias=vec[:, l, V_GLUB + k:V_GLUB + k + 1]).then_inc(read((step, i)), 1)
                if kind == "msplit":
                    for k in range(ND):
                        if k == 0:
                            act.wait_ge(chunk_done, FIRST[("cm", l, "wb2", 3)])
                        act.wait_ge(merged, mrg_no(l, 2, k) + 1)
                        nc.scalar.activation(h_hi[:, k], xm[:, k], ACT.Copy).then_inc(m_hi_done, 1)
                if kind == "outT":
                    half, t = step[1], step[2]
                    src = wait_full(act, (step, 0))
                    nc.scalar.activation(o_tm[:, t, half * S:(half + 1) * S], src[:], ACT.Copy).then_inc(read((step, 0)), 1)

        @block.vector
        def _(dve):
            steps = [0]
            v = nc.vector

            def mark(ins):
                steps[0] += 1
                ins.then_inc(dve_step, 1)
                return steps[0]

            def after(n):
                dve.wait_ge(dve_step, n)

            def then_wait(ins):
                after(mark(ins))

            def reduce_angle(x_, t_):
                then_wait(v.tensor_scalar(t_, x_, INV2PI, MAGIC, ALU.mult, ALU.add))
                then_wait(v.tensor_scalar(t_, t_, MAGIC, None, ALU.subtract))
                for part in (PI_A, PI_B, PI_C):
                    then_wait(v.scalar_tensor_tensor(x_, t_, -part, x_, ALU.mult, ALU.add))
                then_wait(v.tensor_scalar(x_, x_, PI_IN, -PI_IN, ALU.min, ALU.max))

            def rotate(x1, x2, cos_, sin_, shape):
                size = int(np.prod(shape))
                names = "abcd"[:len(shape)]
                ta, tb = (rope[:, i, 0:size].rearrange(f"p ({' '.join(names)}) -> p {' '.join(names)}",
                                                       **dict(zip(names[1:], shape[1:]))) for i in range(2))
                v.tensor_tensor(ta, x1, sin_, ALU.mult)
                last = mark(v.tensor_tensor(tb, x2, sin_, ALU.mult))
                after(last)
                v.tensor_tensor(x1, x1, cos_, ALU.mult)
                last = mark(v.tensor_tensor(x2, x2, cos_, ALU.mult))
                after(last)
                v.tensor_tensor(x1, x1, tb, ALU.subtract)
                return v.tensor_tensor(x2, x2, ta, ALU.add)

            dve.wait_ge(const_in, 16 * 8)
            mark(v.tensor_copy(posf[:], posi[:]))
            after(steps[0])
            then_wait(v.tensor_tensor(sin_t[:], posf[:].unsqueeze(2).broadcast_to([P, NT, 64]),
                                      invf.unsqueeze(1).broadcast_to([P, NT, 64]), ALU.mult))
            reduce_angle(sin_t[:], cos_t[:])
            v.scalar_tensor_tensor(cos_t[:], sin_t[:], -1.0, sin_t[:], ALU.mult, ALU.max).then_inc(ang_ready, 1)
            then_wait(v.tensor_tensor(lbt[:, 4], lbt[:, 0], lbt[:, 1], ALU.max))
            v.tensor_tensor(lbt[:, 2:4], lbt[:, 0:2], lbt[:, 4:5].broadcast_to([P, 2, NW]), ALU.subtract
                            ).then_inc(lb_exp, 1)
            dve.wait_ge(cs_sig, 1)
            v.tensor_tensor(cs[:, 2], cs[:, 0], cs[:, 1], ALU.mult).then_inc(cs_ready, 1)
            dve.wait_ge(rope_tab, 2)
            then_wait(v.tensor_tensor(lbt[:, 5], lbt[:, 2], lbt[:, 3], ALU.add))
            then_wait(v.reciprocal(lbt[:, 5], lbt[:, 5]))
            then_wait(v.tensor_tensor(lbt[:, 2:4], lbt[:, 2:4], lbt[:, 5:6].broadcast_to([P, 2, NW]), ALU.mult))
            then_wait(v.tensor_tensor(lb[:, 0, 0], lbt[:, 2], lbt[:, 2], ALU.subtract))
            then_wait(v.tensor_tensor(lbt[:, 6], lbt[:, 2], lbt[:, 3], ALU.add))
            then_wait(v.tensor_tensor(lb[:, 1, 0], lbt[:, 6], lbt[:, 2], ALU.subtract))
            then_wait(v.tensor_scalar(lb[:, :, 1], lb[:, :, 0], -1.0, 1.0, ALU.mult, ALU.add))

            def s5_layer(l):
                wait_read(dve, (ATT_LAST[l], 2 * HEADS))
                th, ar, t1 = s5s[:, 1], s5s[:, 2], s5s[:, 3]
                a_re, a_im = s5p[:, l, 0], s5p[:, l, 1]
                v.memset(mt, 0.0).then_inc(mt_clear, 1)
                mark(v.memset(m8, 0.0))
                dve.wait_ge(s5_dt, l + 1)
                mark(v.tensor_tensor(ar, a_re, s5s[:, 0], ALU.mult))
                then_wait(v.tensor_tensor(th, a_im, s5s[:, 0], ALU.mult))
                reduce_angle(th, t1)
                ang, lnm, ab = pwt[:, 0], pwt[:, 1], pwt[:, 2]
                by_m = mpow.unsqueeze(2).broadcast_to([P, NPOW, G])
                mark(v.tensor_tensor(lnm, ar.unsqueeze(1).broadcast_to([P, NPOW, G]), by_m, ALU.mult))
                then_wait(v.tensor_tensor(ang, th.unsqueeze(1).broadcast_to([P, NPOW, G]), by_m, ALU.mult))
                reduce_angle(ang, ab)
                mark(v.tensor_copy(s5s[:, 6], ang[:, CH]))
                v.scalar_tensor_tensor(ab, ang, -1.0, ang, ALU.mult, ALU.max).then_inc(s5_ang, 1)
                dve.wait_ge(s5_trig, l + 1)
                mark(v.tensor_copy(s5s[:, 5], lnm[:, CH]))
                mark(v.tensor_tensor(pw[:, 0], pw[:, 0], lnm, ALU.mult))
                then_wait(v.tensor_tensor(pw[:, 1], pw[:, 1], lnm, ALU.mult))
                nr, fr, fi, den, t2 = s5s[:, 7], s5s[:, 8], s5s[:, 9], s5s[:, 10], s5s[:, 11]
                ni = pw[:, 1, 1]
                mark(v.tensor_scalar(nr, pw[:, 0, 1], -1.0, None, ALU.add))
                mark(v.tensor_tensor(den, a_re, a_re, ALU.mult))
                then_wait(v.tensor_tensor(t2, a_im, a_im, ALU.mult))
                then_wait(v.tensor_tensor(den, den, t2, ALU.add))
                mark(v.reciprocal(den, den))
                mark(v.tensor_tensor(fr, nr, a_re, ALU.mult))
                then_wait(v.tensor_tensor(t2, ni, a_im, ALU.mult))
                then_wait(v.tensor_tensor(fr, fr, t2, ALU.add))
                mark(v.tensor_tensor(fr, fr, den, ALU.mult))
                mark(v.tensor_tensor(fi, ni, a_re, ALU.mult))
                then_wait(v.tensor_tensor(t2, nr, a_im, ALU.mult))
                then_wait(v.tensor_tensor(fi, fi, t2, ALU.subtract))
                then_wait(v.tensor_tensor(fi, fi, den, ALU.mult))

            def s5_quarter(l, j, step):
                gs = slice(QG * j, QG * (j + 1))
                fr, fi, mag8, phi = (s5s[:, i, gs] for i in (8, 9, 5, 6))
                if j == 0:
                    dve.wait_ge(par_in, 16 * (l + 1))
                else:
                    wait_full(dve, (("s5", l, j - 1), 6))
                b3 = [P, QG, GC]
                frb, fib = fr.unsqueeze(2).broadcast_to(b3), fi.unsqueeze(2).broadcast_to(b3)
                w1_, w2_ = (wtmp[:, i] for i in range(2))
                sm = [wtmp[:, :, i] for i in range(4)]
                mark(v.tensor_tensor(sm[0], par[:, 0, gs], frb, ALU.mult))
                mark(v.scalar_tensor_tensor(sm[1], par[:, 1, gs], sgn, fib, ALU.mult, ALU.mult))
                mark(v.scalar_tensor_tensor(sm[2], par[:, 1, gs], sgn, frb, ALU.mult, ALU.mult))
                mark(v.tensor_tensor(sm[3], par[:, 0, gs], fib, ALU.mult))
                mark(v.tensor_scalar(cct[:, 0], par[:, 2, gs], sgn, -1.0, ALU.mult, ALU.mult))
                then_wait(v.tensor_scalar(cct[:, 1], par[:, 3, gs], -1.0, None, ALU.mult))
                mark(v.tensor_tensor(bbs[:, 0], sm[0], sm[1], ALU.add))
                then_wait(v.tensor_tensor(bbs[:, 1], sm[2], sm[3], ALU.subtract))

                def combine(out_, re, im, x_, y_, op, n):
                    shape = [P, QG, n, GC]
                    re, im = (a.rearrange("p m g -> p g m").unsqueeze(3).broadcast_to(shape) for a in (re, im))
                    x_, y_ = (a.unsqueeze(2).broadcast_to(shape) for a in (x_, y_))
                    t_ = wtmp[:, :, 0:n]
                    mark(v.tensor_tensor(out_, re, x_, ALU.mult))
                    then_wait(v.tensor_tensor(t_, im, y_, ALU.mult))
                    then_wait(v.tensor_tensor(out_, out_, t_, op))

                combine(ca1, pw[:, 0, :, gs], pw[:, 1, :, gs], cct[:, 0], cct[:, 1], ALU.add, NPOW)
                combine(ca2, pw[:, 0, 1:NPOW, gs], pw[:, 1, 1:NPOW, gs], cct[:, 1], cct[:, 0], ALU.subtract, CH)
                wv = wmat.rearrange("p g (j c) -> p g j c", j=CH)
                combine(wv, pw[:, 0, CH - 1::-1, gs], pw[:, 1, CH - 1::-1, gs], bbs[:, 0], bbs[:, 1], ALU.add, CH)
                v.tensor_copy(m8[:, :, 1:], mag8.unsqueeze(2).broadcast_to([P, QG, NCH - 1])).then_inc(s5_w, 1)
                then_wait(v.tensor_tensor(tang, phi.unsqueeze(2).broadcast_to([P, QG, NCH]),
                                          nidx.unsqueeze(1).broadcast_to([P, QG, NCH]), ALU.mult))
                reduce_angle(tang, tcos)
                v.scalar_tensor_tensor(tcos, tang, -1.0, tang, ALU.mult, ALU.max).then_inc(s5_tab_ang, 1)
                dve.wait_ge(s5_tab, NW * l + j + 1)
                b1, b2 = (wait_full(dve, (step, 4 + q))[:].rearrange("p (g n) -> p g n", g=QG) for q in range(2))
                if l or j:
                    dve.wait_ge(y_saved, 16 * (NW * l + j))
                v.tensor_tensor(zz, b1, tcos, ALU.mult).then_inc(read((step, 4)), 1)
                v.tensor_tensor(tt, b2, tsin, ALU.mult).then_inc(read((step, 5)), 1)
                wait_read(dve, (step, 4))
                wait_read(dve, (step, 5))
                then_wait(v.tensor_tensor(zz, zz, tt, ALU.add))
                flat = [a.rearrange("p g n -> p (g n)") for a in (tt, m8, zz)]
                then_wait(v.tensor_tensor_scan(flat[0], flat[1], flat[2], 0.0, ALU.mult, ALU.add))
                v.tensor_tensor(zz, tt, tcos, ALU.mult)
                v.tensor_tensor(v2, tt, tsin, ALU.mult).then_inc(v_ready, 1)
                dve.wait_ge(v_ready, NW * l + j + 1)

            for step in STEPS:
                kind, l = step[0], step[1]
                name = step[2] if kind in ("cm", "tm") else None
                if kind == "ada" and step[2] == 23:
                    src = wait_full(dve, ("ada", l))
                    then_wait(v.tensor_tensor(mod[:, l], src[:, 0:24], vec[:, l, V_ADAB:V_ADAB + 24], ALU.add))
                    v.tensor_tensor(mod[:, l], src[:, 24:48], mod[:, l], ALU.add).then_inc(read(("ada", l)), 1)
                    wait_read(dve, ("ada", l))
                    v.scalar_tensor_tensor(mod[:, l, 8:16], mod[:, l, 8:16], 1.0, vec[:, l, V_NORM:V_NORM + 8],
                                           ALU.add, ALU.mult).then_inc(mod_ready, 1)
                if kind == "h":
                    dve.wait_ge(r_ready, l + 1)
                    dve.wait_ge(mod_ready, l + 1)

                    def low(k):
                        dve.wait_ge(hhi_done, ND * l + k + 1)
                        v.scalar_tensor_tensor(h_lo[:, k], ht[:, k % 4], mod[:, l, k:k + 1],
                                               h_hi[:, k].bitcast(F32), ALU.add, ALU.subtract).then_inc(h_ready, 1)

                    for k in range(ND):
                        if k >= 4:
                            dve.wait_ge(h_ready, ND * l + k - 3)
                        v.scalar_tensor_tensor(ht[:, k % 4], xm[:, k], mod[:, l, 8 + k:9 + k], rb, ALU.mult, ALU.mult
                                               ).then_inc(t_ready, 1)
                        if k:
                            low(k - 1)
                    low(ND - 1)
                if name == "iq":
                    for t in range(NT):
                        wait_read(dve, (step, t))
                    for t in (0, 2):
                        x_ = tmb[:, t:t + 2].rearrange("p t (h r i) -> p t h r i", h=IH, r=2)
                        shape = [P, 2, IH, 32]
                        last = rotate(x_[:, :, :, 0], x_[:, :, :, 1],
                                      cos_t[:, t:t + 2, ::2].unsqueeze(2).broadcast_to(shape),
                                      sin_t[:, t:t + 2, ::2].unsqueeze(2).broadcast_to(shape), shape[1:])
                        if t == 0:
                            then_wait(last)
                        else:
                            last.then_inc(tm_roped, 1)
                            dve.wait_ge(tm_roped, 4 * l + 1)
                if name == "ikw":
                    for t in range(NT):
                        wait_read(dve, (step, t))
                    x_ = ikd[:, :, 0:128].rearrange("p t (h r i) -> p t h r i", h=2, r=2)
                    shape = [P, NT, 2, 32]
                    rotate(x_[:, :, :, 0], x_[:, :, :, 1],
                           cos_t[:, :, ::2].unsqueeze(2).broadcast_to(shape),
                           sin_t[:, :, ::2].unsqueeze(2).broadcast_to(shape), shape[1:]).then_inc(tm_roped, 1)
                    dve.wait_ge(tm_roped, 4 * l + 2)
                if name == "q":
                    for t in range(NT):
                        wait_read(dve, (step, t))
                        wait_read(dve, (("tm", l, "kv"), t))
                    for t in range(NT):
                        r4 = rope[:, t % 2].rearrange("p (h d) -> p h d", h=HEADS)
                        if t >= 2:
                            after(steps[0])
                        then_wait(v.tensor_tensor(rope[:, t % 2], tmb[:, t], tmb[:, t], ALU.mult))
                        mark(v.tensor_reduce(stat[:, 4 * t:4 * t + 4], r4, AX.X, ALU.add))
                    after(steps[0])
                    k4 = rope[:, 0].rearrange("p (h d) -> p h d", h=NT)
                    then_wait(v.tensor_tensor(k4, kv[:, :, 0:HD], kv[:, :, 0:HD], ALU.mult))
                    v.tensor_reduce(stat[:, 16:20], k4, AX.X, ALU.add).then_inc(ssq_ready, 1)
                    dve.wait_ge(rstd_ready, l + 1)
                    for t in range(NT):
                        mark(v.scalar_tensor_tensor(kv[:, t, 0:HD], kv[:, t, 0:HD], stat[:, 16 + t:17 + t],
                                                    gq[:, l, 1], ALU.mult, ALU.mult))
                    for t in range(NT):
                        for h in range(HEADS):
                            x_ = tmb[:, t, h * HD:(h + 1) * HD]
                            mark(v.scalar_tensor_tensor(x_, x_, stat[:, 4 * t + h:4 * t + h + 1], gq[:, l, 0],
                                                        ALU.mult, ALU.mult))
                    after(steps[0])
                    x_ = kv[:, :, 0:HD].rearrange("p t (r i) -> p t r i", r=2)
                    rotate(x_[:, :, 0], x_[:, :, 1], cos_t[:], sin_t[:], [NT, 64]).then_inc(tm_roped, 1)
                    dve.wait_ge(tm_roped, 4 * l + 3)
                    for t in (0, 2):
                        x_ = tmb[:, t:t + 2].rearrange("p t (h r i) -> p t h r i", h=HEADS, r=2)
                        shape = [P, 2, HEADS, 64]
                        last = rotate(x_[:, :, :, 0], x_[:, :, :, 1],
                                      cos_t[:, t:t + 2].unsqueeze(2).broadcast_to(shape),
                                      sin_t[:, t:t + 2].unsqueeze(2).broadcast_to(shape), shape[1:])
                        if t == 0:
                            then_wait(last)
                        else:
                            last.then_inc(tm_roped, 1)
                            dve.wait_ge(tm_roped, 4 * l + 4)
                if kind == "idx":
                    _, _, b, h = step
                    n = idx_no(l, b, h)
                    keys = (b + 1) * P
                    acc = isc[:, ISC[b]:ISC[b] + keys]
                    wait_read(dve, (step, 0))
                    w_h = ikd[:, b, 128 + h:129 + h]
                    if h:
                        dve.wait_ge(rl_used, n)
                        v.scalar_tensor_tensor(acc, rl[:, n % 2, 0:keys], w_h, acc, ALU.mult, ALU.add
                                               ).then_inc(rl_used, 1)
                    else:
                        v.tensor_scalar(acc, rl[:, n % 2, 0:keys], w_h, None, ALU.mult).then_inc(rl_used, 1)
                if kind == "topk":
                    b = step[2]
                    keys = (b + 1) * P
                    acc = isc[:, ISC[b]:ISC[b] + keys]
                    diag = acc[:, b * P:keys]
                    top = stat[:, 48:56]
                    wk = work[:, 0:keys]
                    dve.wait_ge(rl_used, idx_no(l, b, IH - 1) + 1)
                    then_wait(v.tensor_tensor(diag, diag, cmin, ALU.min))
                    for r in range(TOPK // 8):
                        then_wait(v.max(top, wk if r else acc))
                        then_wait(v.match_replace(wk, top, wk if r else acc, TAKEN))
                    then_wait(v.tensor_scalar(acc, wk, -2e38, NEG_BIG, ALU.is_gt, ALU.mult))
                    v.tensor_tensor(diag, diag, cneg, ALU.min).then_inc(mask_ready, 1)
                if kind == "att":
                    b = step[2]
                    keys = (b + 1) * P
                    if b:
                        wait_read(dve, (("att", l, b - 1), HEADS + b - 1))
                        dve.wait_ge(mask_ready, 3 * l + 4 - b)
                    for h in range(HEADS):
                        src = wait_full(dve, (step, h))
                        bias = isc[:, ISC[b]:ISC[b] + keys] if b else cneg
                        v.scalar_tensor_tensor(logit[:, h, 0:keys], src[:, 0:keys], ATT_SCALE, bias, ALU.mult, ALU.add
                                               ).then_inc(read((step, h)), 1)
                    for h in range(HEADS):
                        wait_read(dve, (step, h))
                    then_wait(v.tensor_reduce(stat[:, 24:28], logit[:, :, 0:keys], AX.X, ALU.max))
                    v.tensor_scalar(stat[:, 32:36], stat[:, 24:28], -1.0, None, ALU.mult).then_inc(neg_ready, 1)
                    dve.wait_ge(exp_ready, HEADS * (NT * l + b + 1))
                    then_wait(v.reciprocal(stat[:, 40:44], stat[:, 36:40]))
                    v.tensor_tensor(logit[:, :, 0:keys], logit[:, :, 0:keys],
                                    stat[:, 40:44].unsqueeze(2).broadcast_to([P, HEADS, keys]), ALU.mult
                                    ).then_inc(p_ready, 1)
                if name == "hf":
                    p = step[3]
                    for i in range(2):
                        hd_ = 2 * p + i
                        wait_read(dve, (step, i))
                        then_wait(v.tensor_scalar(lf[:, i], lf[:, i], lb[:, l, 1, hd_:hd_ + 1],
                                                  lb[:, l, 0, hd_:hd_ + 1], ALU.mult, ALU.add))
                        then_wait(v.tensor_scalar(hk[:, i], lf[:, i], -1.0, 1.0, ALU.mult, ALU.add))
                        v.tensor_scalar(lf[:, i], lf[:, i], 1e-30, None, ALU.max).then_inc(hf_ready, 1)
                    for i in range(2):
                        n = 4 * l + 2 * p + i
                        dve.wait_ge(lf_ready, n + 1)
                        v.tensor_tensor_scan(lf[:, i], reset, lf[:, i], 0.0, ALU.mult, ALU.add).then_inc(b_ready, 1)
                if kind == "hg":
                    p = step[2]
                    if p == 0:
                        mark(v.memset(qp, 0.0))
                        mark(v.memset(kp, 0.0))
                        after(steps[0])

                    def difference(n):
                        m, i = LEVELS[n // 2], n % 2
                        if n >= 2:
                            dve.wait_ge(qk_ready, e_no(l, p, n - 2) + 1)
                        elif p:
                            dve.wait_ge(hr_ready, 2 * (2 * l + p))
                        dve.wait_ge(b_ready, 4 * l + 2 * p + i + 1)
                        view = lf[:, i].rearrange("p (n m) -> p n m", m=2 * m)
                        v.tensor_tensor(dd[:, i].rearrange("p (n m) -> p n m", m=2 * m), view,
                                        view[:, :, m - 1:m].broadcast_to([P, S // (2 * m), 2 * m]), ALU.subtract
                                        ).then_inc(d_ready, 1)

                    def products(n):
                        m, i = LEVELS[n // 2], n % 2
                        dve.wait_ge(e_ready, e_no(l, p, n) + 1)
                        wait_read(dve, (("cm", l, "hq", p), i))
                        kv_, qv_, ev_, k_, q_ = (a.rearrange("p (n m) -> p n m", m=2 * m) for a in
                                                 (kp[:, i], qp[:, i], dd[:, i], hk[:, i], hq[:, i]))
                        v.tensor_tensor(kv_[:, :, 0:m], k_[:, :, 0:m], ev_[:, :, 0:m], ALU.mult)
                        v.tensor_tensor(qv_[:, :, m:2 * m], q_[:, :, m:2 * m], ev_[:, :, m:2 * m], ALU.mult
                                        ).then_inc(qk_ready, 1)

                    def level(n):
                        m, i = n // 2, n % 2
                        src = wait_full(dve, (step, 2 + n))
                        wait_read(dve, (step, n))
                        v.copy_predicated(sct[:, i].rearrange("p (c t) -> p c t", c=NT),
                                          msk[:, m].bitcast(I32).unsqueeze(1).broadcast_to([P, NT, P]),
                                          src[:].rearrange("p (c t) -> p c t", c=NT)).then_inc(read((step, 2 + n)), 1)

                    difference(0)
                    difference(1)
                    for i in range(2):
                        src = wait_full(dve, (step, i))
                        v.tensor_tensor(sct[:, i].rearrange("p (c t) -> p c t", c=NT),
                                        src[:].rearrange("p (c t) -> p c t", c=NT),
                                        ident.unsqueeze(1).broadcast_to([P, NT, P]), ALU.mult
                                        ).then_inc(read((step, i)), 1)
                    for n in range(2 * len(LEVELS)):
                        if n >= 2:
                            level(n - 2)
                        products(n)
                        if n + 2 < 2 * len(LEVELS):
                            difference(n + 2)
                    for i in range(2):
                        dve.wait_ge(qk_ready, e_no(l, p, 12 + i) + 1)
                        view = lf[:, i].rearrange("p (n m) -> p n m", m=P)
                        v.tensor_tensor(dd[:, i].rearrange("p (n m) -> p n m", m=P), view,
                                        view[:, :, P - 1:P].broadcast_to([P, NT, P]), ALU.subtract
                                        ).then_inc(d_ready, 1)
                    for i in range(2):
                        level(12 + i)
                    for i in range(2):
                        dve.wait_ge(e_ready, e_no(l, p, 14 + 2 * i) + 1)
                        v.tensor_tensor(kp[:, i], hk[:, i], dd[:, i], ALU.mult).then_inc(qk_ready, 1)
                        dve.wait_ge(e_ready, e_no(l, p, 15 + 2 * i) + 1)
                        v.tensor_tensor(qp[:, i], hq[:, i], lf[:, i], ALU.mult).then_inc(qk_ready, 1)
                    for c in range(3):
                        for i in range(2):
                            src = wait_full(dve, (step, HG_ST + 2 * c + i))
                            if c == 0:
                                ins = v.tensor_copy(st[:, i, 0], src[:, 0:P])
                            else:
                                wait_read(dve, (step, HG_ST + 2 * (c - 1) + i))
                                ins = v.scalar_tensor_tensor(st[:, i, c], st[:, i, c - 1],
                                                             lf[:, i, c * P + P - 1:c * P + P], src[:, 0:P],
                                                             ALU.mult, ALU.add)
                            ins.then_inc(read((step, HG_ST + 2 * c + i)), 1)
                    for i in range(2):
                        src = wait_full(dve, (step, HG_O + i))
                        dve.wait_ge(hr_ready, 2 * (2 * l + p) + i + 1)
                        v.scalar_tensor_tensor(hq[:, i], src[:], vec[:, l, V_ONORM:V_ONORM + 1], dd[:, i],
                                               ALU.mult, ALU.mult).then_inc(read((step, HG_O + i)), 1)
                if kind == "cm" and name in ("hg", "ag", "sg"):
                    j = step[3]
                    branch = {"hg": 0, "ag": 1, "sg": 2}[name]
                    for i in range(2):
                        n, k = gate_no(l, branch, 2 * j + i), 2 * j + i
                        src = wait_full(dve, (step, i))
                        dve.wait_ge(sig_ready, n + 1)
                        if n >= 2:
                            dve.wait_ge(y_done, n - 1)
                        if name == "sg":
                            dve.wait_ge(glu_used, NW * (l + 1))
                        v.tensor_tensor(prod[:, n % 2], src[:], sig[:, sig_no(l, name, k) % 2], ALU.mult
                                        ).then_inc(read((step, i)), 1)
                        wait_read(dve, (step, i))
                        if name == "hg":
                            wait_read(dve, (("hg", l, j), HG_O + i))
                            pre = hq[:, i]
                        elif name == "ag":
                            wait_read(dve, (ATT_LAST[l], 2 * HEADS))
                            pre = o_att[:, k]
                        else:
                            dve.wait_ge(glu_used, NW * l + k + 1)
                            pre = y_g[:, k]
                        v.tensor_tensor(prod[:, n % 2], prod[:, n % 2], pre, ALU.mult).then_inc(prod_ready, 1)
                        if k == 0:
                            y_unused(dve, l, name)
                        dve.wait_ge(y_hi_done, n + 1)
                        v.tensor_tensor(y_lo[:, k], prod[:, n % 2], y_hi[:, k].bitcast(F32), ALU.subtract
                                        ).then_inc(y_done, 1)
                if kind == "cm" and name[:2] == "wb":
                    branch, j = int(name[2]), step[3]
                    for i in range(2):
                        k = 2 * j + i
                        wait_read(dve, (("cm", l, f"mg{branch}", j), i))
                        src = wait_full(dve, (step, i))
                        sg_ = sig[:, sig_no(l, f"mg{branch}", k) % 2]
                        if branch == 0:
                            if k == 0:
                                dve.wait_ge(x_saved, 16 * (l + 1))
                            v.tensor_tensor(xm[:, k], src[:], sg_, ALU.mult).then_inc(read((step, i)), 1)
                            continue
                        if k == 0:
                            dve.wait_ge(y_done, gate_no(l, branch, 3) + 1)
                        if k >= 2:
                            dve.wait_ge(merged, mrg_no(l, branch, k - 2) + 1)
                        v.tensor_tensor(prod[:, k % 2], src[:], sg_, ALU.mult).then_inc(read((step, i)), 1)
                        wait_read(dve, (step, i))
                        v.tensor_tensor(xm[:, k], xm[:, k], prod[:, k % 2], ALU.add).then_inc(merged, 1)
                if kind == "s5":
                    if step[2] == 0:
                        s5_layer(l)
                    s5_quarter(l, step[2], step)
                if kind == "gelu":
                    for k in range(NW):
                        n = NW * l + k
                        dve.wait_ge(ycm_in, 16 * QG * (n + 1))
                        v.scalar_tensor_tensor(y_g[:, k].rearrange("p (n j) -> p j n", j=CH),
                                               up[:, k].rearrange("p (j n) -> p j n", j=CH),
                                               vec[:, l, V_D + k:V_D + k + 1],
                                               y_cm[:, k].rearrange("p (j n) -> p j n", j=CH), ALU.mult, ALU.add
                                               ).then_inc(gl_sq, 1)
                    for k in range(NW):
                        n = NW * l + k
                        dve.wait_ge(gl_arg, 2 * n + 1)
                        then_wait(v.tensor_scalar(prod[:, k % 2], prod[:, k % 2], 0.044715, 1.0, ALU.mult, ALU.add))
                        v.tensor_tensor(prod[:, k % 2], prod[:, k % 2], y_g[:, k], ALU.mult).then_inc(gl_sig, 1)
                        dve.wait_ge(gl_arg, 2 * n + 2)
                        v.tensor_tensor(y_g[:, k], y_g[:, k], prod[:, k % 2], ALU.mult).then_inc(gl_split, 1)
                        dve.wait_ge(gl_hi, n + 1)
                        v.tensor_tensor(y_lo[:, k], y_g[:, k], y_hi[:, k].bitcast(F32), ALU.subtract
                                        ).then_inc(gl_lo, 1)
                if name == "glu":
                    for i in range(2):
                        k = 2 * step[3] + i
                        wait_read(dve, (step, i))
                        v.tensor_tensor(y_g[:, k], y_g[:, k], prod[:, k % 2], ALU.mult).then_inc(glu_used, 1)
                if kind == "msplit":
                    for k in range(ND):
                        dve.wait_ge(m_hi_done, ND * l + k + 1)
                        v.tensor_tensor(h_lo[:, k], xm[:, k], h_hi[:, k].bitcast(F32), ALU.subtract
                                        ).then_inc(m_done, 1)
                if name == "wo":
                    for i in range(2):
                        k = 2 * step[3] + i
                        src = wait_full(dve, (step, i))
                        dve.wait_ge(x_back_in, 16 * (l + 1))
                        v.scalar_tensor_tensor(xm[:, k], src[:], mod[:, l, 16 + k:17 + k], x_back[:, k],
                                               ALU.mult, ALU.add).then_inc(read((step, i)), 1)

        @block.tensor
        def _(pe):
            mm = nc.tensor.matmul

            def three(out_, a_hi, a_lo, b_hi, b_lo, first, last):
                mm(out_, a_hi, b_hi, start=first, stop=False)
                mm(out_, a_hi, b_lo, start=False, stop=False)
                return mm(out_, a_lo, b_hi, start=False, stop=last)

            def split_chunk(n):
                m = SPLIT_NO[n]
                pe.wait_ge(lo_done, m + 1)
                return w_hi[:, m % SPLIT_SLOTS], w_lo[:, m % SPLIT_SLOTS]

            pe.wait_ge(const_in, 16 * 8)
            for step in STEPS:
                kind, l = step[0], step[1]
                if kind == "xT":
                    k = step[1]
                    if k == 0:
                        pe.wait_ge(x_in, 16 * NT)
                    dst = wait_free(pe, (step, 0))
                    for t in range(NT):
                        last = nc.tensor.transpose(dst[:, t * P:(t + 1) * P], x_tm[:, t, k * P:(k + 1) * P], ident)
                    last.then_inc(full((step, 0)), 1)
                if kind == "ada":
                    c = step[2]
                    n = FIRST[step]
                    if c == 0:
                        wait_free(pe, ("ada", l))
                        pe.wait_ge(cs_ready, 1)
                    kh = c % 2
                    pe.wait_ge(raw_full[n % RAW_SLOTS], 16 * (n // RAW_SLOTS + 1))
                    for ct in range(2):
                        col = 24 * kh + 2 * (c // 2) + ct
                        for kk in range(KC):
                            last = mm(bank[7][:, col:col + 1], raw[:, n % RAW_SLOTS, kk, ct * P:(ct + 1) * P],
                                      cs[:, 2, KC * kh + kk:KC * kh + kk + 1], start=kk == 0, stop=kk == KC - 1)
                    last.then_inc(chunk_done, 1)
                if kind == "h":
                    dst = wait_free(pe, (step, 0))
                    for k in range(ND):
                        pe.wait_ge(sq_ready, ND * l + k + 1)
                        last = mm(dst[:], ones, sq[:, k % 2], start=k == 0, stop=k == ND - 1)
                        if k < ND - 1:
                            last.then_inc(sq_used, 1)
                    last.then_inc(full((step, 0)), 1)
                if kind == "tm":
                    n = FIRST[step]
                    for c0 in range(0, COLS[step[2]][1], NCOL):
                        for kh in range(2):
                            wh, wl = split_chunk(n)
                            width = CHUNKS[n][0][4]
                            pe.wait_ge(h_ready, ND * l + KC * kh + KC)
                            for t in range(NT):
                                dst = bank[t]
                                if c0 == 0 and kh == 0:
                                    wait_free(pe, (step, t))
                                for kk in range(KC):
                                    k = KC * kh + kk
                                    ts = slice(t * P, (t + 1) * P)
                                    last = three(dst[:, c0:c0 + width], h_hi[:, k, ts], h_lo[:, k, ts],
                                                 wh[:, kk, 0:width], wl[:, kk, 0:width],
                                                 kh == 0 and kk == 0, kh == 1 and kk == KC - 1)
                            last.then_inc(chunk_done, 1)
                            n += 1
                if kind == "cm":
                    name, j = step[2], step[3]
                    n = FIRST[step]
                    halves = len(chunks_of(step))
                    if name == "glu":
                        pe.wait_ge(gl_lo, NW * (l + 1))
                    elif name[:2] == "wb":
                        pe.wait_ge(y_done, gate_no(l, int(name[2]), 3) + 1)
                    for kh in range(halves):
                        wh, wl = split_chunk(n + kh)
                        for ct in range(2):
                            dst = wait_free(pe, (step, ct)) if kh == 0 else bank[BANKS.uses[(step, ct)][0]]
                            for kk in range(KC):
                                k = KC * kh + kk
                                if name == "wo":
                                    pe.wait_ge(m_done, ND * l + k + 1)
                                x_hi, x_lo = (y_hi, y_lo) if halves == 1 else (h_hi, h_lo)
                                cols = slice(ct * P, (ct + 1) * P)
                                last = three(dst[:], wh[:, kk, cols], wl[:, kk, cols], x_hi[:, k], x_lo[:, k],
                                             k == 0, kh == halves - 1 and kk == KC - 1)
                        last.then_inc(chunk_done, 1)
                if kind in ("ikT", "kT"):
                    pe.wait_ge(tm_roped, 4 * l + (2 if kind == "ikT" else 3))
                    dst = wait_free(pe, (step, 0))
                    for t in range(NT):
                        src = ikd[:, t, 0:P] if kind == "ikT" else kv[:, t, 0:HD]
                        last = nc.tensor.transpose(dst[:, t * P:(t + 1) * P], src, ident)
                    last.then_inc(full((step, 0)), 1)
                if kind in ("iqT", "qT"):
                    t = step[2]
                    pe.wait_ge(tm_roped, 4 * l + (1 if kind == "iqT" else 4))
                    dst = wait_free(pe, (step, 0))
                    for h in range(NT):
                        last = nc.tensor.transpose(dst[:, h * P:(h + 1) * P], tmb[:, t, h * P:(h + 1) * P], ident)
                    last.then_inc(full((step, 0)), 1)
                if kind == "idx":
                    _, _, b, h = step
                    if h == 0:
                        wait_read(pe, (("ikT", l), 0))
                        wait_read(pe, (("iqT", l, b), 0))
                    dst = wait_free(pe, (step, 0))
                    ps = slice(IDIM * (h % 2), IDIM * (h % 2) + IDIM)
                    mm(dst[:, 0:(b + 1) * P], iq_t[ps, h // 2, b * P:(b + 1) * P], ik_t[ps, 0:(b + 1) * P],
                       start=True, stop=True).then_inc(full((step, 0)), 1)
                if kind == "att":
                    b = step[2]
                    keys = (b + 1) * P
                    wait_read(pe, (("kT", l), 0))
                    wait_read(pe, (("qT", l, b), 0))
                    for h in range(HEADS):
                        dst = wait_free(pe, (step, h))
                        mm(dst[:, 0:keys], q_t[:, h, b * P:keys], k_t[:, 0:keys], start=True, stop=True
                           ).then_inc(full((step, h)), 1)
                    pe.wait_ge(p_ready, NT * l + b + 1)
                    for s_ in range(b + 1):
                        dst = wait_free(pe, (step, HEADS + s_))
                        for h in range(HEADS):
                            last = nc.tensor.transpose(dst[:, h * P:(h + 1) * P], logit[:, h, s_ * P:(s_ + 1) * P], ident)
                        last.then_inc(full((step, HEADS + s_)), 1)
                    dst = wait_free(pe, (step, HEADS + b + 1))
                    for s_ in range(b + 1):
                        wait_read(pe, (step, HEADS + s_))
                        last = mm(dst[:], kv[:, s_, HD:2 * HD], p_t[:, s_], start=s_ == 0, stop=s_ == b)
                    last.then_inc(full((step, HEADS + b + 1)), 1)
                if kind == "hg":
                    p = step[2]
                    for n in range(2 + 2 * len(LEVELS)):
                        i = n % 2
                        k_, q_ = (hk, hq) if n < 2 else (kp, qp)
                        if n < 2:
                            pe.wait_ge(b_ready, 4 * l + 2 * p + i + 1)
                            wait_read(pe, (("cm", l, "hq", p), i))
                        else:
                            pe.wait_ge(qk_ready, e_no(l, p, n - 2) + 1)
                        dst = wait_free(pe, (step, n))
                        for c in range(NT):
                            cs_ = slice(c * P, (c + 1) * P)
                            last = mm(dst[:, cs_], k_[:, i, cs_], q_[:, i, cs_], start=True, stop=True)
                        last.then_inc(full((step, n)), 1)
                    for i in range(2):
                        pe.wait_ge(qk_ready, e_no(l, p, 14 + 2 * i) + 1)
                        dst = wait_free(pe, (step, HG_KT + i))
                        for c in range(NT - 1):
                            cs_ = slice(c * P, (c + 1) * P)
                            last = nc.tensor.transpose(dst[:, cs_], kp[:, i, cs_], ident)
                        last.then_inc(full((step, HG_KT + i)), 1)
                    pe.wait_ge(qk_ready, e_no(l, p, 17) + 1)
                    for c in range(NT):
                        for i in range(2):
                            vh = hv[:, c, (2 * p + i) * HD:(2 * p + i + 1) * HD]
                            cs_ = slice(c * P, (c + 1) * P)
                            if c < NT - 1:
                                wait_read(pe, (step, HG_KT + i))
                                dst = wait_free(pe, (step, HG_ST + 2 * c + i))
                                mm(dst[:, 0:P], kdt[:, i, c], vh, start=True, stop=True
                                   ).then_inc(full((step, HG_ST + 2 * c + i)), 1)
                        for i in range(2):
                            vh = hv[:, c, (2 * p + i) * HD:(2 * p + i + 1) * HD]
                            cs_ = slice(c * P, (c + 1) * P)
                            if c == 0:
                                wait_read(pe, (step, 14 + i))
                                dst = wait_free(pe, (step, HG_O + i))
                            dst = bank[BANKS.uses[(step, HG_O + i)][0]]
                            last = mm(dst[:, cs_], vh, sct[:, i, cs_], start=True, stop=c == 0)
                            if c:
                                wait_read(pe, (step, HG_ST + 2 * (c - 1) + i))
                                last = mm(dst[:, cs_], st[:, i, c - 1], qp[:, i, cs_], start=False, stop=True)
                            if c == NT - 1:
                                last.then_inc(full((step, HG_O + i)), 1)
                    for i in range(2):
                        pe.wait_ge(hsq_ready, 2 * (2 * l + p) + i + 1)
                        dst = wait_free(pe, (step, HG_SS + i))
                        mm(dst[:], ones, hk[:, i], start=True, stop=True).then_inc(full((step, HG_SS + i)), 1)
                if kind == "s5":
                    j = step[2]
                    q_no = NW * l + j
                    pe.wait_ge(s5_w, q_no + 1)
                    for q in range(2):
                        dst = wait_free(pe, (step, q))
                        for g in range(4):
                            last = mm(dst[0:GC, g * P:(g + 1) * P], bbs[:, 0, 4 * q + g],
                                      ca1[:, 4 * q + g, 0:CH].rearrange("p m c -> p (m c)"), start=True, stop=True)
                        last.then_inc(full((step, q)), 1)
                    for q in range(2):
                        dst = wait_free(pe, (step, 2 + q))
                        for g in range(4):
                            last = nc.tensor.transpose(dst[:, g * P:(g + 1) * P], wmat[:, 4 * q + g], ident)
                        last.then_inc(full((step, 2 + q)), 1)
                    pe.wait_ge(u_in, 16 * CH * (q_no + 1))
                    wait_read(pe, (step, 2))
                    wait_read(pe, (step, 3))
                    for q, w_ in enumerate((wt1, wt2)):
                        dst = wait_free(pe, (step, 4 + q))
                        for g in range(QG):
                            last = mm(dst[:, g * NCH:(g + 1) * NCH], w_[:, g], u_j[:, g], start=True, stop=True)
                        last.then_inc(full((step, 4 + q)), 1)
                    pe.wait_ge(mt_in, 16 * CH * (q_no + 1))
                    pe.wait_ge(v_ready, q_no + 1)
                    dst = wait_free(pe, (step, 6))
                    for g in range(QG):
                        a_ = g * NCH
                        mm(dst[:, a_:a_ + NCH], mt[:, g], u_j[:, g], start=True, stop=False)
                        mm(dst[:, a_ + 1:a_ + NCH], ca1[:, g, 1:NPOW].rearrange("p m c -> p (m c)"),
                           zz[:, g, 0:NCH - 1], start=False, stop=False)
                        last = mm(dst[:, a_ + 1:a_ + NCH], ca2[:, g].rearrange("p m c -> p (m c)"),
                                  v2[:, g, 0:NCH - 1], start=False, stop=True)
                    last.then_inc(full((step, 6)), 1)
                if kind == "outT":
                    half, t = step[1], step[2]
                    for k in range(4):
                        wait_x(pe, DEPTH, 4 * half + k)
                    dst = wait_free(pe, (step, 0))
                    for k in range(4):
                        last = nc.tensor.transpose(dst[:, k * P:(k + 1) * P],
                                                   xm[:, 4 * half + k, t * P:(t + 1) * P], ident)
                    last.then_inc(full((step, 0)), 1)


_OUT = (1, S, D)


def laid_out(inputs):
    a = {k: np.asarray(v) for k, v in inputs.items()}
    wb = a["w_branch"]
    source = {"ada_w": a["ada_w"], "w_in": a["w_in"], "wb0": wb[:, 0], "wb1": wb[:, 1], "wb2": wb[:, 2],
              "s5_glu_w": a["s5_glu_w"], "w_out": a["w_out"]}

    def chunk(n):
        (name, l, k0, c0, width), _ = CHUNKS[n]
        w = source[name][l, k0 * P:(k0 + KC) * P, c0:c0 + width]
        return w.reshape(KC, P, width).transpose(1, 0, 2)

    wfull = np.stack([chunk(n) for n in FULL])
    wnarrow = np.stack([chunk(n) for n in NARROW])

    def cm(v):
        v = v.reshape(*v.shape[:-1], -1, P)
        return np.moveaxis(v, -1, 0)

    vecs = np.concatenate([cm(a[k]) for k in ("ada_b", "norm_g", "hg_onorm_g", "s5_d", "s5_glu_b")], axis=-1)
    gains = np.broadcast_to(np.stack([a["at_qnorm_g"], a["at_knorm_g"]], axis=1), (P, DEPTH, 2, HD))
    twice = lambda v: np.concatenate([v, v], axis=0)
    s5v = np.stack([twice(np.moveaxis(a["s5_a_re"], -1, 0)), twice(np.moveaxis(a["s5_a_im"], -1, 0)),
                    np.broadcast_to(a["s5_log_dt"], (P, DEPTH, G))], axis=2)
    b_re, b_im = (np.moveaxis(a[k], 2, 1) for k in ("s5_b_re", "s5_b_im"))
    c_re, c_im = (np.moveaxis(a[k], 3, 1) for k in ("s5_c_re", "s5_c_im"))
    s5m = np.stack([np.concatenate(pair, axis=1) for pair in
                    ((b_re, b_im), (b_im, b_re), (c_re, c_im), (c_im, c_re))], axis=2)

    consts = np.zeros((P, CONST_COLS), np.float32)
    i = np.arange(P)
    consts[:, 0:128] = np.eye(P)
    consts[:, 128:256] = 1
    consts[:, 256:768] = (np.arange(S) % P != 0)
    consts[:, 768:832] = np.float32(10000.0) ** (-np.arange(0, HD, 2, dtype=np.float32) / np.float32(HD))
    consts[:, 832:896] = np.arange(NCH)
    consts[:, 896:1024] = np.where(i[None] <= i[:, None], 3e38, NEG_BIG)
    consts[:, 1024:1152] = np.where(i[None] <= i[:, None], 0, NEG_BIG)
    consts[:, 1152] = np.where(i < SP_, -1, 1)
    consts[:, 1153:1162] = np.arange(NPOW)
    consts[:, 1162] = HALF_PI
    consts[:, 1163] = EPS
    masks = np.zeros((P, len(LEVELS), P), np.float32)
    for n, m in enumerate(LEVELS):
        s_, t_ = i[:, None], i[None]
        masks[:, n] = (s_ // (2 * m) == t_ // (2 * m)) & (s_ % (2 * m) < m) & (t_ % (2 * m) >= m)
    return {
        "wfull": wfull, "wnarrow": wnarrow, "x": a["x"].reshape(S, D), "cvec": cm(a["c"])[:, 0],
        "pos": a["positions"].reshape(NT, P).T, "lblog": cm(a["hg_lb_logits"]), "vecs": vecs, "gains": gains,
        "s5v": s5v, "s5m": s5m, "consts": consts, "masks": masks,
    }


def kernel(**inputs):
    import concourse.bacc as bacc
    from concourse.bass_utils import run_bass_kernel_spmd

    nc = bacc.Bacc("TRN2", target_bir_lowering=False, num_devices=1, dynamic_dma_scratch_size=4096)
    arrays, args = {}, []
    for name, value in laid_out(inputs).items():
        value = np.ascontiguousarray(value)
        arrays[f"in_{name}"] = value
        args.append(nc.dram_tensor(f"in_{name}", value.shape, mybir.dt.from_np(value.dtype),
                                   kind="ExternalInput").ap())
    out = nc.dram_tensor("out", (S, D), F32, kind="ExternalOutput").ap()
    program(nc, *args, out)
    r = run_bass_kernel_spmd(nc, [arrays], core_ids=[0])
    return r.results[0]["out"].reshape(_OUT)
```
